# Optimizing a Trainium2 kernel written in Bass

```python
import math
import jax, jax.numpy as jnp
from jax import lax
import numpy as np

D_MODEL = 1024
BATCH = 1
SEQ = 256
DEPTH = 2

GRID_W = 64
HEAD_DIM = 64
QB = 128
N_BRANCH = 4
BRANCH_W = 256
A_HEADS = 4
A_KV_HEADS = 2
B_HEADS = 4
NA_ROWS = 8
NA_COLS = 16
C_HEADS = 4
C_KV_HEADS = 2
WINDOW = 128
D_HEADS = 4
MLA_Q_RANK = 192
MLA_KV_RANK = 128
MLA_NOPE = 64
MLA_ROPE = 32
MLA_V = 64
D_FF = 4 * D_MODEL
ROPE_THETA = 10000.0
EPS = 1e-6

IN_SPLITS = (
    A_HEADS * HEAD_DIM, A_KV_HEADS * HEAD_DIM, A_KV_HEADS * HEAD_DIM,
    B_HEADS * HEAD_DIM, B_HEADS * HEAD_DIM, B_HEADS * HEAD_DIM,
    C_HEADS * HEAD_DIM, C_KV_HEADS * HEAD_DIM, C_KV_HEADS * HEAD_DIM,
    MLA_Q_RANK, MLA_KV_RANK, MLA_ROPE,
)
IN_W = sum(IN_SPLITS)

kernel_name = "hybrid_gated_parallel_encoder"

def rms_norm(x, g):
    x32 = x.astype(jnp.float32)
    y = x32 * lax.rsqrt(jnp.mean(x32 * x32, axis=-1, keepdims=True) + EPS)
    return y.astype(x.dtype) * g

def rope(x, pos):
    d = x.shape[-1]
    half = d // 2
    inv = jnp.power(ROPE_THETA, -jnp.arange(half, dtype=jnp.float32) / half)
    ang = pos.astype(jnp.float32)[:, None] * inv
    ang = ang.reshape((ang.shape[0],) + (1,) * (x.ndim - 3) + (half,))
    c, s = jnp.cos(ang).astype(x.dtype), jnp.sin(ang).astype(x.dtype)
    x1, x2 = x[..., :half], x[..., half:]
    return jnp.concatenate([x1 * c - x2 * s, x2 * c + x1 * s], axis=-1)

def axial_rope(x, row, col):
    half = x.shape[-1] // 2
    return jnp.concatenate([rope(x[..., :half], row), rope(x[..., half:], col)], axis=-1)

def global_attention(q, k, v, scale):
    B, S, Hk, G, dq = q.shape
    nb = S // QB
    qb = q.reshape(B, nb, QB, Hk, G, dq).transpose(1, 0, 2, 3, 4, 5)

    def one(qblk):
        s = jnp.einsum('bqkgd,bskd->bkgqs', qblk, k).astype(jnp.float32) * scale
        p = jax.nn.softmax(s, axis=-1).astype(v.dtype)
        return jnp.einsum('bkgqs,bskd->bqkgd', p, v)

    o = lax.map(one, qb)
    return o.transpose(1, 0, 2, 3, 4, 5).reshape(B, S, Hk * G * v.shape[-1])

def neighbourhood_attention(q, k, v, rel_bias):
    B, S, H, hd = q.shape
    rows = S // GRID_W
    wr, wc = min(NA_ROWS, rows), NA_COLS
    nk = wr * wc
    t = jnp.arange(S, dtype=jnp.int32)
    r, c = t // GRID_W, t % GRID_W
    rs = jnp.clip(r - wr // 2, 0, rows - wr)
    cs = jnp.clip(c - wc // 2, 0, GRID_W - wc)
    kr = rs[:, None] + jnp.arange(wr, dtype=jnp.int32)
    kc = cs[:, None] + jnp.arange(wc, dtype=jnp.int32)
    idx = (kr[:, :, None] * GRID_W + kc[:, None, :]).reshape(S, nk)
    dr = kr - r[:, None] + (NA_ROWS - 1)
    dc = kc - c[:, None] + (NA_COLS - 1)
    bidx = (dr[:, :, None] * (2 * NA_COLS - 1) + dc[:, None, :]).reshape(S, nk)
    table = rel_bias.reshape(H, -1).astype(jnp.float32)
    nb = S // QB
    qb = q.reshape(B, nb, QB, H, hd).transpose(1, 0, 2, 3, 4)
    scale = hd ** -0.5

    def one(args):
        qblk, ib, bb = args
        kg, vg = k[:, ib], v[:, ib]
        s = jnp.einsum('bqhd,bqkhd->bhqk', qblk, kg).astype(jnp.float32) * scale
        s = s + table[:, bb][None]
        p = jax.nn.softmax(s, axis=-1).astype(v.dtype)
        return jnp.einsum('bhqk,bqkhd->bqhd', p, vg)

    o = lax.map(one, (qb, idx.reshape(nb, QB, nk), bidx.reshape(nb, QB, nk)))
    return o.transpose(1, 0, 2, 3, 4).reshape(B, S, H * hd)

def window_sink_attention(q, k, v, sink):
    B, S, Hk, G, hd = q.shape
    nb = S // QB
    qb = q.reshape(B, nb, QB, Hk, G, hd)

    def bands(a):
        ap = jnp.pad(a, ((0, 0), (QB, QB), (0, 0), (0, 0))).reshape(B, nb + 2, QB, Hk, a.shape[-1])
        return jnp.concatenate([ap[:, :-2], ap[:, 1:-1], ap[:, 2:]], axis=2)

    kb, vb = bands(k), bands(v)
    s = jnp.einsum('bnqkgd,bnskd->bnkgqs', qb, kb).astype(jnp.float32) * (hd ** -0.5)
    i = jnp.arange(QB, dtype=jnp.int32)
    l = jnp.arange(3 * QB, dtype=jnp.int32)
    diff = i[:, None] - l[None, :] + QB
    kpos = (jnp.arange(nb, dtype=jnp.int32)[:, None] - 1) * QB + l[None, :]
    mask = (jnp.abs(diff) <= WINDOW)[None] & ((kpos >= 0) & (kpos < S))[:, None, :]
    slopes = jnp.exp2(-8.0 * jnp.arange(1, Hk * G + 1, dtype=jnp.float32) / (Hk * G))
    alibi = -slopes.reshape(Hk, G)[:, :, None, None] * jnp.abs(diff).astype(jnp.float32)
    s = jnp.where(mask[None, :, None, None], s + alibi, -jnp.inf)
    sk = jnp.broadcast_to(sink.reshape(Hk, G)[:, :, None, None].astype(jnp.float32), s.shape[:-1] + (1,))
    p = jax.nn.softmax(jnp.concatenate([s, sk], axis=-1), axis=-1)[..., :-1].astype(v.dtype)
    o = jnp.einsum('bnkgqs,bnskd->bnqkgd', p, vb)
    return o.reshape(B, S, Hk * G * hd)

def setup_inputs(seed: int = 0) -> dict:
    key = jax.random.key(seed)
    ks = jax.random.split(key, 24)

    def nrm(k, shape, scale):
        return jax.random.normal(k, shape, jnp.float32) * scale

    D = D_MODEL
    return {
        "x": nrm(ks[0], (BATCH, SEQ, D), 1.0),
        "norm1_g": 1.0 + nrm(ks[1], (DEPTH, D), 0.05),
        "w_in": nrm(ks[2], (DEPTH, D, IN_W), D ** -0.5),
        "w_gate": nrm(ks[3], (DEPTH, D, N_BRANCH * D), D ** -0.5),
        "b_gate": nrm(ks[4], (DEPTH, N_BRANCH * D), 0.1),
        "a_q_norm_g": 1.0 + nrm(ks[5], (DEPTH, HEAD_DIM), 0.05),
        "a_k_norm_g": 1.0 + nrm(ks[6], (DEPTH, HEAD_DIM), 0.05),
        "b_rel_bias": nrm(ks[7], (DEPTH, B_HEADS, 2 * NA_ROWS - 1, 2 * NA_COLS - 1), 0.5),
        "c_sink": nrm(ks[8], (DEPTH, C_HEADS), 0.5),
        "d_q_norm_g": 1.0 + nrm(ks[9], (DEPTH, MLA_Q_RANK), 0.05),
        "d_kv_norm_g": 1.0 + nrm(ks[10], (DEPTH, MLA_KV_RANK), 0.05),
        "d_w_uq": nrm(ks[11], (DEPTH, MLA_Q_RANK, D_HEADS * (MLA_NOPE + MLA_ROPE)), MLA_Q_RANK ** -0.5),
        "d_w_ukv": nrm(ks[12], (DEPTH, MLA_KV_RANK, D_HEADS * (MLA_NOPE + MLA_V)), MLA_KV_RANK ** -0.5),
        "w_branch": nrm(ks[13], (DEPTH, N_BRANCH, BRANCH_W, D), BRANCH_W ** -0.5),
        "w_o": nrm(ks[14], (DEPTH, D, D), D ** -0.5),
        "norm2_g": 1.0 + nrm(ks[15], (DEPTH, D), 0.05),
        "w_ff1": nrm(ks[16], (DEPTH, D, D_FF), D ** -0.5),
        "w_ff2": nrm(ks[17], (DEPTH, D_FF, D), D_FF ** -0.5),
        "final_g": 1.0 + nrm(ks[18], (D,), 0.05),
    }

def reference(x, norm1_g, w_in, w_gate, b_gate, a_q_norm_g, a_k_norm_g, b_rel_bias,
              c_sink, d_q_norm_g, d_kv_norm_g, d_w_uq, d_w_ukv, w_branch, w_o,
              norm2_g, w_ff1, w_ff2, final_g):
    B, S, D = x.shape
    t = jnp.arange(S, dtype=jnp.int32)
    row, col = t // GRID_W, t % GRID_W
    cuts = np.cumsum(IN_SPLITS)[:-1].tolist()
    for l in range(DEPTH):
        h = rms_norm(x, norm1_g[l])
        (aq, ak, av, bq, bk, bv, cq, ck, cv,
         c_q, c_kv, k_rope) = jnp.split(h @ w_in[l], cuts, axis=-1)

        aq = rms_norm(aq.reshape(B, S, A_HEADS, HEAD_DIM), a_q_norm_g[l])
        ak = rms_norm(ak.reshape(B, S, A_KV_HEADS, HEAD_DIM), a_k_norm_g[l])
        aq = axial_rope(aq.reshape(B, S, A_KV_HEADS, A_HEADS // A_KV_HEADS, HEAD_DIM), row, col)
        ak = axial_rope(ak, row, col)
        o_a = global_attention(aq, ak, av.reshape(B, S, A_KV_HEADS, HEAD_DIM), HEAD_DIM ** -0.5)

        o_b = neighbourhood_attention(bq.reshape(B, S, B_HEADS, HEAD_DIM),
                                      bk.reshape(B, S, B_HEADS, HEAD_DIM),
                                      bv.reshape(B, S, B_HEADS, HEAD_DIM), b_rel_bias[l])

        o_c = window_sink_attention(cq.reshape(B, S, C_KV_HEADS, C_HEADS // C_KV_HEADS, HEAD_DIM),
                                    ck.reshape(B, S, C_KV_HEADS, HEAD_DIM),
                                    cv.reshape(B, S, C_KV_HEADS, HEAD_DIM), c_sink[l])

        qd = (rms_norm(c_q, d_q_norm_g[l]) @ d_w_uq[l]).reshape(B, S, D_HEADS, MLA_NOPE + MLA_ROPE)
        q_nope, q_rot = qd[..., :MLA_NOPE], rope(qd[..., MLA_NOPE:], t)
        kvd = (rms_norm(c_kv, d_kv_norm_g[l]) @ d_w_ukv[l]).reshape(B, S, D_HEADS, MLA_NOPE + MLA_V)
        k_nope, vd = kvd[..., :MLA_NOPE], kvd[..., MLA_NOPE:]
        k_rot = jnp.broadcast_to(rope(k_rope[:, :, None, :], t), (B, S, D_HEADS, MLA_ROPE))
        qd = jnp.concatenate([q_nope, q_rot], axis=-1)[:, :, :, None, :]
        kd = jnp.concatenate([k_nope, k_rot], axis=-1)
        o_d = global_attention(qd, kd, vd, (MLA_NOPE + MLA_ROPE) ** -0.5)

        br = jnp.stack([o_a, o_b, o_c, o_d], axis=2)
        y = jnp.einsum('bsnc,ncd->bsnd', br, w_branch[l])
        g = jax.nn.sigmoid(h @ w_gate[l] + b_gate[l]).reshape(B, S, N_BRANCH, D)
        x = x + jnp.sum(g * y, axis=2) @ w_o[l]

        h2 = rms_norm(x, norm2_g[l])
        x = x + jnp.square(jax.nn.relu(h2 @ w_ff1[l])) @ w_ff2[l]
    return rms_norm(x, final_g)


_drawn_inputs = setup_inputs


def setup_inputs(seed=0):
    import zlib

    import numpy as np

    out = dict(_drawn_inputs(seed))
    spreads = {}
    factors = {'b_gate': 4.381,
     'a_q_norm_g': 8.0,
     'a_k_norm_g': 8.0,
     'c_sink': 8.0,
     'd_q_norm_g': 8.0,
     'd_kv_norm_g': 6.391}
    for name, (base, spread) in spreads.items():
        noise = np.random.default_rng([zlib.crc32(name.encode()), seed]).standard_normal(out[name].shape)
        drawn = base * np.exp(spread * noise) if base else spread * noise
        out[name] = __import__('jax').numpy.asarray(drawn.astype(out[name].dtype))
    for name, factor in factors.items():
        out[name] = (out[name] * factor).astype(out[name].dtype)
    return out
```

```python
from contextlib import ExitStack

import numpy as np

import concourse.bass as bass
from concourse import mybir

F32 = mybir.dt.float32
F32R = mybir.dt.float32r
ALU = mybir.AluOpType
ACT = mybir.ActivationFunctionType
AX = mybir.AxisListType.X

P = 128
D = 1024
SEQ = 256
T = SEQ // P
KD = D // P
DEPTH = 2
GRID_W = 64
ROWS = SEQ // GRID_W
HD = 64
H = 4
NB = 4
NA_ROWS, NA_COLS = 8, 16
BIAS_ROW = 2 * NA_COLS - 1
WINDOW = 128
QR, KVR, ROPE = 192, 128, 32
DQ = HD + ROPE
D_FF = 4 * D
EPS = 1e-6
MASKED = -1e30

AQ, AK, AV, BQ, BK, BV, CQ, CK, CV, DCQ, DCKV, DKR, IN_W = np.cumsum(
    [0, 256, 128, 128, 256, 256, 256, 256, 128, 128, QR, KVR, ROPE]).tolist()

IN_N = 8
IN_C = IN_W // IN_N
GATE_N = 4 * NB
Y_AFTER = {3 * n + 6: n for n in range(NB - 1)}
FF_N = D_FF // 256
CHUNKS = [("in", j) for j in range(IN_N)]
for _i in range(GATE_N):
    CHUNKS.append(("gate", _i))
    if _i in Y_AFTER:
        CHUNKS.append(("y", Y_AFTER[_i]))
CHUNKS += [("y", NB - 1)] + [("o", c) for c in range(4)] + [("f1", 0)]
for _i in range(FF_N - 1):
    CHUNKS += [("f1", _i + 1), ("f2", _i)]
CHUNKS.append(("f2", FF_N - 1))
NC = len(CHUNKS)
POS = {name: c for c, name in enumerate(CHUNKS)}
RAW, RING = 2, 4
AHEAD = 3
WMAX = KD * IN_C
assert NC % RING == 0 and NC % RAW == 0
MLP_LOOP = POS["f1", 1]
MLP_TURNS = (FF_N - 2) // 2

W_JOBS = []
for _i in range(GATE_N):
    W_JOBS.append(("gate", _i, 0))
    if _i in Y_AFTER:
        W_JOBS += [("y", Y_AFTER[_i], q) for q in range(4)]
W_JOBS += [("y", NB - 1, q) for q in range(4)]
W_AT = {job: k for k, job in enumerate(W_JOBS)}

HEADS = [(n, hh if n % 2 else (hh % 2) * 2 + hh // 2, hh // 2, hh % 2) for n in range(NB) for hh in range(H)]
NH = len(HEADS)

STEPS = POS["y", NB - 1] + 1
SCORES, SOFTMAX, TURN, VALUES, HEAD_OUT = 7, 8, 9, 10, 11

X_AT = {
    "aq": (6, 0), "ak": (6, 1), "bq": (7, 1), "bk": (8, 1), "cq": (9, 1), "ck": (10, 1),
    "lq": (11, 1), "lkv": (12, 1), "uq0": (15, 0), "uq1": (15, 1), "ukv0": (16, 0), "ukv1": (16, 1),
    "dq0": (18, 1), "dk0": (19, 0), "dq1": (19, 1), "dk1": (20, 0),
}
X_JOBS = list(X_AT)
X_STEP = {at: name for name, at in X_AT.items()}
NX = len(X_JOBS)

G1, G2, BG, GQ, GKV = 0, KD, 2 * KD, 2 * KD + NB * KD, 2 * KD + NB * KD + 2
NCOL = GKV + 1
VECTORS = {G1: KD, G2: KD, BG: NB * KD, GQ: 1, GQ + 1: 1, GKV: 1}

C_ID = 0
C_RA = C_ID + P
C_RD = C_RA + 2 * T * HD
C_DIST = C_RD + 2 * T * ROPE
C_WIN = C_DIST + T * SEQ
C_FLIP = C_WIN + GRID_W
C_N = C_FLIP + P

WARM = (6, 4, 2)

DVE_LINKS, POOL_LINKS = 50, 12


def constants():
    tok = np.arange(SEQ)

    def rot(pos, half):
        inv = np.power(np.float32(10000.0), -np.arange(half, dtype=np.float32) / np.float32(half))
        ang = (pos.astype(np.float32)[:, None] * inv).astype(np.float32).astype(np.float64)
        c, s = np.cos(ang).astype(np.float32), np.sin(ang).astype(np.float32)
        return np.concatenate([c, c], 1), np.concatenate([-s, s], 1)

    rc, rs = rot(tok // GRID_W, HD // 4)
    cc, cs = rot(tok % GRID_W, HD // 4)
    dc, ds = rot(tok, ROPE // 2)
    dist = np.abs(tok[:, None] - tok[None, :]).astype(np.float32)
    dist[dist > WINDOW] = -MASKED
    col = np.arange(P) % GRID_W
    first = np.clip(col[::-1] - NA_COLS // 2, 0, GRID_W - NA_COLS)[:, None]
    kc = np.arange(GRID_W)[None, :]
    window = np.where((kc >= first) & (kc < first + NA_COLS), 0.0, MASKED).astype(np.float32)

    def tiles(a):
        return a.reshape(T, P, -1).transpose(1, 0, 2).reshape(P, -1)

    parts = [np.eye(P, dtype=np.float32), tiles(np.concatenate([rc, cc], 1)), tiles(np.concatenate([rs, cs], 1)),
             tiles(dc), tiles(ds), tiles(dist), window, np.eye(P, dtype=np.float32)[::-1] * HD ** 0.5]
    table = np.ascontiguousarray(np.concatenate(parts, 1), dtype=np.float32)
    assert table.shape == (P, C_N)
    return table


def trunk_kernel(nc, x, norm1_g, w_in, w_gate, b_gate, a_q_norm_g, a_k_norm_g, b_rel_bias, c_sink,
                 d_q_norm_g, d_kv_norm_g, d_w_uq, d_w_ukv, w_branch, w_o, norm2_g, w_ff1, w_ff2, final_g,
                 table, out):
    ctx = ExitStack()
    with ctx:
        def sb(name, shape, dt=F32):
            return ctx.enter_context(nc.sbuf_tensor(name, shape, dt))

        def ps(name, shape):
            return ctx.enter_context(nc.psum_tensor(name, shape, F32))

        def sem(name):
            return ctx.enter_context(nc.semaphore(name))

        raw = sb("raw", [P, RAW, WMAX])
        w_hi = sb("w_hi", [P, RING, WMAX], F32R)
        w_lo = sb("w_lo", [P, RING, WMAX], F32R)
        xs = sb("xs", [P, T, D])
        act_hi = sb("act_hi", [P, KD, SEQ], F32R)
        act_lo = sb("act_lo", [P, KD, SEQ], F32R)
        qkv = sb("qkv", [P, T, IN_W])
        big = sb("big", [P, 8, 512])
        h = big[:, 0:4, :].rearrange("p a b -> p (a b)").rearrange("p (t d) -> p t d", t=T)
        relu = [big[:, 4 + b, :] for b in range(2)]
        sq = [big[:, 6 + b, :] for b in range(2)]
        bias = sb("bias", [P, H, T * SEQ])
        bias_flat = bias[:, :, :].rearrange("p a b -> p (a b)")
        qd = bias_flat[:, 0:T * H * DQ].rearrange("p (t h d) -> p t h d", t=T, h=H)
        kd = bias_flat[:, T * H * DQ:2 * T * H * DQ].rearrange("p (t h d) -> p t h d", t=T, h=H)
        part_hi = sb("part_hi", [P, 2, 2, SEQ], F32R)
        part_lo = sb("part_lo", [P, 2, 2, SEQ], F32R)
        qk_ab = sb("qk_ab", [P, 8, SEQ])
        qk_c = sb("qk_c", [P, 3, SEQ])
        qT = {0: qk_ab[:, 0:2, :], 1: qk_ab[:, 3:5, :], 2: qk_c[:, 0:2, :], 3: qk_ab[:, 0:4, :]}
        kT = {0: qk_ab[:, 2:3, :], 1: qk_ab[:, 5:7, :], 2: qk_c[:, 2:3, :], 3: qk_ab[:, 4:8, :]}
        prob = sb("prob", [P, 2, T, SEQ])
        probT = sb("probT", [P, 2, T, SEQ])
        mix = sb("mix", [P, 4, 512])
        scratch = mix[:, :, :].rearrange("p a b -> p (a b)")
        tmp = sb("tmp", [P, 2, 512])
        vd = sb("vd", [P, T, H, HD])
        cq_order = vd[:, :, :, :].rearrange("p t h d -> p t (h d)")
        latT = sb("latT", [P, 3, SEQ])
        w_uq = sb("w_uq", [P, 2, H * DQ])
        w_ukv = sb("w_ukv", [P, H * 2 * HD])
        cst = sb("cst", [P, C_N])
        vec_rows = sb("vec_rows", [DEPTH * NCOL, P])
        vec_all = sb("vec_all", [P, DEPTH * NCOL])
        vec = sb("vec", [P, NCOL])
        gain_qk = sb("gain_qk", [P, 2, HD])
        sink = sb("sink", [P, H])
        nsink = sb("nsink", [P, H])
        warm = sb("warm", [P, 1])
        mean = sb("mean", [P, T, 2])
        rstd = sb("rstd", [P, T])
        ss_a = sb("ss_a", [P, T, 6])
        rs_a = sb("rs_a", [P, T, 6])
        ss_d = sb("ss_d", [P, T, 2])
        rs_d = sb("rs_d", [P, T, 2])
        neg_half = sb("neg_half", [P, T * 6])
        neg_one = sb("neg_one", [P, H])
        eps = sb("eps", [P, T * 6])
        inv_head = sb("inv_head", [P, T * 6])
        inv_rank = sb("inv_rank", [P, T, 2])
        top = sb("top", [P, 2, T])
        ntop = sb("ntop", [P, 2, T])
        psum_p = sb("psum_p", [P, 2, T])
        esink = sb("esink", [P, 2, T])
        rsum = sb("rsum", [P, 2, T])
        krot = sb("krot", [P, T, ROPE])

        ident = cst[:, C_ID:C_ID + P]
        cos_a, sin_a = (cst[:, C_RA + k * T * HD:C_RA + (k + 1) * T * HD].rearrange("p (t d) -> p t d", t=T)
                        for k in range(2))
        cos_d, sin_d = (cst[:, C_RD + k * T * ROPE:C_RD + (k + 1) * T * ROPE].rearrange("p (t d) -> p t d", t=T)
                        for k in range(2))
        dist = cst[:, C_DIST:C_DIST + T * SEQ]
        flip = cst[:, C_FLIP:C_FLIP + P]
        window = cst[:, C_WIN:C_WIN + GRID_W]

        bank_w = ps("bank_w", [P, 2, 512])
        bank_acc = ps("bank_acc", [P, 4, 512])
        bank_o = ps("bank_o", [P, 512])
        bank_x = ps("bank_x", [P, 512])
        turn_banks = [bank_o[:, :], bank_x[:, :], bank_acc[:, 0, :], bank_acc[:, 1, :]]

        landed = [sem(f"landed{r}") for r in range(RAW)]
        w_hi_ready = sem("w_hi_ready")
        w_lo_ready = sem("w_lo_ready")
        w_used = sem("w_used")
        x_landed = [sem(f"x_landed{t}") for t in range(T)]
        ident_landed = sem("ident_landed")
        cst_landed = sem("cst_landed")
        rows_landed = sem("rows_landed")
        d_rows_landed = sem("d_rows_landed")
        rows_clear = sem("rows_clear")
        rows_turned = sem("rows_turned")
        half_ready = sem("half_ready")
        x_ready = sem("x_ready")
        mean_ready = sem("mean_ready")
        rstd_ready = sem("rstd_ready")
        h_ready = sem("h_ready")
        h_right_ready = sem("h_right_ready")
        h_turned = sem("h_turned")
        h_hi_ready = sem("h_hi_ready")
        h_lo_ready = sem("h_lo_ready")
        in_half = sem("in_half")
        in_act = sem("in_act")
        in_dve = sem("in_dve")
        gains_landed = sem("gains_landed")
        sink_landed = sem("sink_landed")
        lat_landed = sem("lat_landed")
        bias_landed = sem("bias_landed")
        bias_ready = sem("bias_ready")
        nsink_ready = sem("nsink_ready")
        ss_a_ready = sem("ss_a_ready")
        rs_a_ready = sem("rs_a_ready")
        ss_d_ready = sem("ss_d_ready")
        rs_d_ready = sem("rs_d_ready")
        a_ready = sem("a_ready")
        lat_ready = sem("lat_ready")
        cq_ready = sem("cq_ready")
        d_ready = sem("d_ready")
        x_turned = sem("x_turned")
        x_evac = sem("x_evac")
        gate_tanh = sem("gate_tanh")
        scored = sem("scored")
        top_ready = sem("top_ready")
        exp_ready = sem("exp_ready")
        prob_ready = sem("prob_ready")
        prob_turned = sem("prob_turned")
        probT_ready = sem("probT_ready")
        pv_done = sem("pv_done")
        o_hi_ready = sem("o_hi_ready")
        o_lo_ready = sem("o_lo_ready")
        y_done = sem("y_done")
        y_read = sem("y_read")
        mixed = sem("mixed")
        mix_hi_ready = sem("mix_hi_ready")
        mix_lo_ready = sem("mix_lo_ready")
        acc_done = sem("acc_done")
        relu_ready = sem("relu_ready")
        u_squared = sem("u_squared")
        u_hi_ready = sem("u_hi_ready")
        u_lo_ready = sem("u_lo_ready")
        dve_link = sem("dve_link")
        pool_link = sem("pool_link")
        final_g_landed = sem("final_g_landed")
        stored = sem("stored")

        def f32(ap):
            return ap.bitcast(F32)

        def chunk_cols(c):
            return WMAX if CHUNKS[c][0] == "in" else 2048

        def split_view(buf, c):
            return buf[:, c % RING, 0:chunk_cols(c)]

        def k_view(buf, c, k):
            return split_view(buf, c).rearrange("p (k n) -> p k n", k=k)

        def lo_count(l, c, g=0):
            return l * NC + 4 * g + (c + 1 + RAW)

        def used_count(l, c, g=0):
            return l * NC + 4 * g + (c + 1 + RING)

        block = ctx.enter_context(nc.Block())

        @block.sync
        def _(sp):
            for t in range(T):
                sp.dma_start(xs[:, t, :], x[0, t * P:(t + 1) * P, :]).then_inc(x_landed[t], 16)

            def halves(c, l, g=0):
                kind, i = CHUNKS[c]
                dst = raw[:, c % RAW, 0:chunk_cols(c)]
                if kind in ("in", "gate", "f1"):
                    w, n = {"in": (w_in, IN_C), "gate": (w_gate, 256), "f1": (w_ff1, 256)}[kind]
                    dst = dst.rearrange("p (k n) -> p k n", k=KD)
                    src = w.rearrange("l (k p) (c n) -> l c p k n", p=P, n=n)[bass.ds(l, 1), bass.ds(i + 2 * g, 1)]
                    src = src.rearrange("o a p k n -> (o a p) k n")
                    return [(dst[:, s:s + 4, :], src[:, s:s + 4, :]) for s in (0, 4)]
                dst = dst.rearrange("p (k n) -> p k n", k=2)
                if kind == "y":
                    order = "l m (k b p) n -> l m b p k n" if i % 2 else "l m (b k p) n -> l m b p k n"
                    src = w_branch.rearrange(order, b=2, k=2)[:, i][bass.ds(l, 1)]
                    src = src.rearrange("o b p k n -> (o b) p k n")
                    return [(dst[b * HD:(b + 1) * HD, :, :], src[b]) for b in range(2)]
                w = {"o": w_o, "f2": w_ff2}[kind]
                src = w.rearrange("l (c k p) n -> l c p k n", p=P, k=2)[bass.ds(l, 1), bass.ds(i + 2 * g, 1)]
                src = src.rearrange("o a p k n -> (o a p) k n")
                return [(dst[:, k, :], src[:, k, :]) for k in range(2)]

            def load(c, l, g=0):
                sp.wait_ge(w_lo_ready, l * NC + 4 * g + (c + 1))
                for dst, src in halves(c, l, g):
                    sp.dma_start(dst, src).then_inc(landed[c % RAW], 16)

            with sp.Fori(0, DEPTH) as l:
                for c in range(MLP_LOOP):
                    load(c, l)
                with sp.Fori(0, MLP_TURNS) as g:
                    for c in range(MLP_LOOP, MLP_LOOP + 4):
                        load(c, l, g)
                for c in range(MLP_LOOP + 4 * MLP_TURNS, NC):
                    load(c, l)

            for t in range(T):
                for m in range(2):
                    sp.wait_ge(h_ready, 2 * T * DEPTH + 2 * t + m + 1)
                    half = slice(m * 512, (m + 1) * 512)
                    sp.dma_start(out[0, t * P:(t + 1) * P, half], h[:, t, half]).then_inc(stored, 16)
            sp.wait_ge(stored, 16 * T * 2)

        @block.gpsimd
        def _(pool):
            link = [0]

            def chained(ins, l):
                link[0] += 1
                ins.then_inc(pool_link, 1)
                pool.wait_ge(pool_link, l * POOL_LINKS + (link[0]))

            nc.gpsimd.memset(neg_half[:, :], -0.5)
            nc.gpsimd.memset(neg_one[:, :], -1.0)
            nc.gpsimd.memset(eps[:, :], EPS)
            nc.gpsimd.memset(inv_head[:, :], 1.0 / HD)
            nc.gpsimd.memset(inv_rank[:, :, 0:1], 1.0 / QR)
            nc.gpsimd.memset(inv_rank[:, :, 1:2], 1.0 / KVR).then_inc(half_ready, 1)
            pool.wait_ge(half_ready, 1)
            pool.wait_ge(rows_clear, 1)
            for at, a, b in ((GQ, 0, P), (GQ + 1, P, QR)):
                pool.dma_start(vec_rows[DEPTH * at:DEPTH * (at + 1), 0:b - a], d_q_norm_g[:, a:b]).then_inc(d_rows_landed, 16)
            pool.dma_start(vec_rows[DEPTH * GKV:DEPTH * (GKV + 1), :], d_kv_norm_g).then_inc(d_rows_landed, 16)
            pool.dma_start(cst[:, C_ID + P:], table[:, C_ID + P:]).then_inc(cst_landed, 16)

            def inverse_root(dst, src, inv_width, l):
                n = src.shape[-1]
                chained(nc.gpsimd.tensor_tensor(src, src, inv_width, ALU.mult), l)
                chained(nc.gpsimd.tensor_tensor(src, src, eps[:, 0:n], ALU.add), l)
                return nc.gpsimd.tensor_tensor(dst, src, neg_half[:, 0:n], ALU.pow)

            def norm(k, l):
                for t in range(T):
                    left, right = (mean[:, t, m:m + 1] for m in range(2))
                    pool.wait_ge(mean_ready, 2 * (k * T) + (2 * t + 1))
                    chained(nc.gpsimd.tensor_tensor(left, left, eps[:, 0:1], ALU.add), l)
                    pool.wait_ge(mean_ready, 2 * (k * T) + (2 * t + 2))
                    chained(nc.gpsimd.tensor_tensor(left, left, right, ALU.add), l)
                    nc.gpsimd.tensor_tensor(rstd[:, t:t + 1], left, neg_half[:, 0:1], ALU.pow).then_inc(rstd_ready, 1)

            with pool.Fori(0, DEPTH) as l:
                norm(2 * l, l)
                pool.dma_start(gain_qk[:, 0, :], a_q_norm_g[bass.ds(l, 1), :].to_broadcast([P, HD])).then_inc(gains_landed, 16)
                pool.dma_start(gain_qk[:, 1, :], a_k_norm_g[bass.ds(l, 1), :].to_broadcast([P, HD])).then_inc(gains_landed, 16)
                pool.dma_start(sink[:, :], c_sink[bass.ds(l, 1), :].to_broadcast([P, H])).then_inc(sink_landed, 16)
                uq = d_w_uq[bass.ds(l, 1)].rearrange("o k n -> (o k) n")
                pool.dma_start(w_uq[:, 0, :], uq[0:P, :]).then_inc(lat_landed, 16)
                pool.dma_start(w_uq[0:QR - P, 1, :], uq[P:QR, :]).then_inc(lat_landed, 16)
                pool.dma_start(w_ukv[:, :], d_w_ukv[bass.ds(l, 1)].rearrange("o k n -> (o k) n")).then_inc(lat_landed, 16)
                pool.wait_ge(sink_landed, l * 16 + 16)
                nc.gpsimd.tensor_tensor(nsink[:, :], sink[:, :], neg_one[:, :], ALU.mult).then_inc(nsink_ready, 1)
                pool.wait_ge(ss_a_ready, l + 1)
                inverse_root(rs_a[:, :, :].rearrange("p t h -> p (t h)"), ss_a[:, :, :].rearrange("p t h -> p (t h)"),
                             inv_head[:, :], l).then_inc(rs_a_ready, 1)
                for hd in range(H):
                    for t in range(T):
                        for r in range(2):
                            row = 2 * t + 1 - r
                            at = (NA_ROWS - 1 - row) * BIAS_ROW + NA_COLS - 1 - (GRID_W - 1)
                            table_h = b_rel_bias[bass.ds(l, 1), hd]
                            src = bass.AP(tensor=table_h.tensor, offset=table_h.offset + at,
                                          ap=[[1, GRID_W], [BIAS_ROW, ROWS], [1, GRID_W]])
                            dst = bias[r * GRID_W:(r + 1) * GRID_W, hd, t * SEQ:(t + 1) * SEQ].rearrange(
                                "p (r c) -> p r c", c=GRID_W)
                            pool.dma_start(dst, src).then_inc(bias_landed, 16)
                pool.wait_ge(cst_landed, 16)
                pool.wait_ge(bias_landed, l * (16 * H * T * 2) + 16 * H * T * 2)
                rows = bias_flat.rearrange("p (r c) -> p r c", c=GRID_W)
                nc.gpsimd.tensor_tensor(rows, rows, window.unsqueeze(1).to_broadcast([P, H * T * ROWS, GRID_W]),
                                        ALU.add).then_inc(bias_ready, 1)
                pool.wait_ge(ss_d_ready, l + 1)
                inverse_root(rs_d[:, :, :].rearrange("p t h -> p (t h)"), ss_d[:, :, :].rearrange("p t h -> p (t h)"),
                             inv_rank[:, :, :].rearrange("p t h -> p (t h)"), l).then_inc(rs_d_ready, 1)
                for k in range(4 * (NB - 1)):
                    pool.wait_ge(y_read, l * 16 + (k + 5))
                    if k >= 4:
                        pool.wait_ge(mixed, l * 12 + (k - 3))
                    nc.gpsimd.tensor_tensor(mix[:, k % 4, :], mix[:, k % 4, :], tmp[:, k % 2, :], ALU.add).then_inc(mixed, 1)
                norm(2 * l + 1, l)
                used = link[0]
            assert used == POOL_LINKS, used
            pool.dma_start(scratch[:, 0:D], final_g.rearrange("(o d) -> o d", o=1).to_broadcast([P, D])).then_inc(final_g_landed, 16)
            link[0] = 0
            norm(2 * DEPTH, DEPTH)

        @block.scalar
        def _(act):
            act.dma_start(ident, table[:, C_ID:C_ID + P]).then_inc(ident_landed, 16)
            act.wait_ge(rows_clear, 1)
            for v, at, n in ((norm1_g, G1, KD), (norm2_g, G2, KD), (b_gate, BG, NB * KD)):
                rows = vec_rows[DEPTH * at:DEPTH * (at + n), :]
                act.dma_start(rows, v.rearrange("l (k p) -> (l k) p", p=P)).then_inc(rows_landed, 16)
            nc.scalar.activation(warm[:, :], warm[:, :], ACT.Exp)

            def split_hi(c, l, g=0):
                if c >= NC:
                    return
                act.wait_ge(landed[c % RAW], l * (NC // RAW * 32) + g * 64 + (c // RAW + 1) * 32)
                act.wait_ge(w_used, l * NC + 4 * g + (c + 1))
                nc.scalar.activation(split_view(w_hi, c), raw[:, c % RAW, 0:chunk_cols(c)],
                                     ACT.Copy).then_inc(w_hi_ready, 1)

            def square_sum(k, parts):
                for t, m in parts:
                    act.wait_ge(x_ready, 2 * (k * T) + (2 * t + m + 1))
                    half = slice(m * 512, (m + 1) * 512)
                    nc.scalar.activation(h[:, t, half], xs[:, t, half], ACT.Square, scale=float(D) ** -0.5,
                                         accum_out=mean[:, t, m:m + 1]).then_inc(mean_ready, 1)

            def scale_right(k, t):
                act.wait_ge(rstd_ready, k * T + (t + 1))
                nc.scalar.activation(h[:, t, 512:D], xs[:, t, 512:D], ACT.Copy,
                                     scale=rstd[:, t:t + 1]).then_inc(h_right_ready, 1)

            def turned_hi(k, gain):
                for kc in range(KD):
                    act.wait_ge(h_turned, k * 4 + (kc // 2 + 1))
                    src = turn_banks[kc // 2][:, (kc % 2) * SEQ:(kc % 2 + 1) * SEQ]
                    nc.scalar.activation(act_hi[:, kc, :], src, ACT.Copy,
                                         scale=vec[:, gain + kc:gain + kc + 1]).then_inc(h_hi_ready, 1)

            def evac(step, l):
                name = X_STEP.get(step)
                if name is None:
                    return
                act.wait_ge(x_turned, l * NX + (X_JOBS.index(name) + 1))
                x2 = bank_x[:, :].rearrange("p (b s) -> p b s", b=2)
                if name in ("aq", "bq", "cq"):
                    ins = nc.scalar.activation(qT["abc".index(name[0])], x2, ACT.Copy)
                elif name == "bk":
                    ins = nc.scalar.activation(kT[1], x2, ACT.Copy)
                elif name in ("ak", "ck"):
                    ins = nc.scalar.activation(kT["abc".index(name[0])][:, 0, :], x2[:, 0, :], ACT.Copy)
                elif name == "lq":
                    nc.scalar.activation(latT[:, 0, :], x2[:, 0, :], ACT.Copy, scale=vec[:, GQ:GQ + 1])
                    ins = nc.scalar.activation(latT[0:QR - P, 1, :], x2[0:QR - P, 1, :], ACT.Copy,
                                               scale=vec[0:QR - P, GQ + 1:GQ + 2])
                elif name == "lkv":
                    ins = nc.scalar.activation(latT[:, 2, :], x2[:, 0, :], ACT.Copy, scale=vec[:, GKV:GKV + 1])
                elif name in ("uq0", "uq1"):
                    t = int(name[-1])
                    ins = nc.scalar.activation(qd[:, t, :, :].rearrange("p h d -> p (h d)"), bank_x[:, 0:H * DQ], ACT.Copy)
                elif name in ("ukv0", "ukv1"):
                    t = int(name[-1])
                    kv = bank_x[:, :].rearrange("p (h m d) -> p h m d", h=H, m=2)
                    nc.scalar.activation(kd[:, t, :, 0:HD], kv[:, :, 0, :], ACT.Copy)
                    ins = nc.scalar.activation(vd[:, t, :, :], kv[:, :, 1, :], ACT.Copy)
                else:
                    to = (qT if name[1] == "q" else kT)[3]
                    b = int(name[-1])
                    ins = nc.scalar.activation(to[0:DQ, 2 * b:2 * b + 2, :], x2[0:DQ, :, :], ACT.Copy)
                ins.then_inc(x_evac, 1)

            def exps(i, l):
                n, hd, _, _ = HEADS[i]
                b = i % 2
                act.wait_ge(top_ready, l * NH + (i + 1))
                if i >= 2:
                    act.wait_ge(prob_turned, l * NH + (i - 1))
                if n == 2:
                    act.wait_ge(sink_landed, l * 16 + 16)
                    nc.scalar.activation(esink[:, b, :], ntop[:, b, :], ACT.Exp, bias=sink[:, hd:hd + 1])
                scale = (DQ if n == 3 else HD) ** -0.5
                for t in range(T):
                    ins = nc.scalar.activation(prob[:, b, t, :], bank_acc[:, b, t * SEQ:(t + 1) * SEQ], ACT.Exp,
                                               bias=ntop[:, b, t:t + 1], scale=scale, accum_out=psum_p[:, b, t:t + 1])
                ins.then_inc(exp_ready, 1)

            def probT_evac(i, l):
                b = i % 2
                act.wait_ge(prob_turned, l * NH + (i + 1))
                if i >= 2:
                    act.wait_ge(pv_done, l * NH + (i - 1))
                nc.scalar.activation(probT[:, b, :, :].rearrange("p t s -> p (t s)"), bank_acc[:, 2 + b, :],
                                     ACT.Copy).then_inc(probT_ready, 1)

            def heads_hi(i, l):
                n, _, blk, half = HEADS[i]
                if half == 0:
                    return
                act.wait_ge(pv_done, l * NH + (i + 1))
                if n >= 2:
                    act.wait_ge(w_used, used_count(l, POS["y", n - 2]))
                nc.scalar.activation(part_hi[:, n % 2, blk, :], bank_o[:, blk * SEQ:(blk + 1) * SEQ],
                                     ACT.Copy).then_inc(o_hi_ready, 1)

            def gate(i, l):
                act.wait_ge(w_used, used_count(l, POS["gate", i]))
                if i >= 8:
                    act.wait_ge(y_read, l * 16 + (i - 7))
                bank = bank_w[:, W_AT["gate", i, 0] % 2, :]
                for d in range(2):
                    ins = nc.scalar.activation(big[:, i % 8, d * SEQ:(d + 1) * SEQ], bank[:, d * SEQ:(d + 1) * SEQ],
                                               ACT.Tanh, bias=vec[:, BG + 2 * i + d:BG + 2 * i + d + 1], scale=0.5)
                ins.then_inc(gate_tanh, 1)

            def mlp(i, l, g=0):
                b = i % 2
                act.wait_ge(w_used, used_count(l, POS["f1", i], g))
                nc.scalar.activation(relu[b], bank_w[:, b, :], ACT.Relu).then_inc(relu_ready, 1)
                act.wait_ge(relu_ready, l * FF_N + 2 * g + (i + 1))
                nc.scalar.activation(part_hi[:, b, :, :].rearrange("p k s -> p (k s)"), relu[b],
                                     ACT.Square).then_inc(u_hi_ready, 1)

            with act.Fori(0, DEPTH) as l:
                square_sum(2 * l, ((0, 0), (0, 1), (1, 0)))
                split_hi(0, l)
                square_sum(2 * l, ((1, 1),))
                scale_right(2 * l, 0)
                scale_right(2 * l, 1)
                turned_hi(2 * l, G1)
                split_hi(1, l)
                split_hi(2, l)
                for s in range(STEPS):
                    kind, j = CHUNKS[s]
                    if 0 <= s - HEAD_OUT < NH:
                        heads_hi(s - HEAD_OUT, l)
                    if 0 <= s - VALUES < NH:
                        probT_evac(s - VALUES, l)
                    evac((s, 0), l)
                    if 0 <= s - SOFTMAX < NH:
                        exps(s - SOFTMAX, l)
                    if kind == "in":
                        act.wait_ge(in_half, l * IN_N + (j + 1))
                        nc.scalar.activation(qkv[:, 0, j * IN_C:(j + 1) * IN_C], bank_w[:, 0, 0:IN_C],
                                             ACT.Copy).then_inc(in_act, 1)
                    split_hi(s + AHEAD, l)
                    if kind == "gate":
                        gate(j, l)
                    evac((s, 1), l)
                for q in range(4):
                    act.wait_ge(mixed, l * 12 + (8 + q + 1))
                    nc.scalar.activation(act_hi[:, 2 * q:2 * q + 2, :].rearrange("p k s -> p (k s)"), mix[:, q, :],
                                         ACT.Copy, scale=0.5).then_inc(mix_hi_ready, 1)
                split_hi(POS["o", 3], l)
                split_hi(POS["f1", 0], l)
                square_sum(2 * l + 1, ((0, 0), (0, 1)))
                split_hi(POS["f1", 1], l)
                scale_right(2 * l + 1, 0)
                square_sum(2 * l + 1, ((1, 0), (1, 1)))
                scale_right(2 * l + 1, 1)
                turned_hi(2 * l + 1, G2)
                split_hi(POS["f2", 0], l)
                mlp(0, l)
                with act.Fori(0, MLP_TURNS) as g:
                    for i in (1, 2):
                        split_hi(POS["f1", i] + AHEAD - 1, l, g)
                        mlp(i, l, g)
                        split_hi(POS["f2", i - 1] + AHEAD - 1, l, g)
                split_hi(POS["f2", FF_N - 1], l)
                mlp(FF_N - 1, l)
            square_sum(2 * DEPTH, ((0, 0), (0, 1), (1, 0), (1, 1)))

        @block.vector
        def _(dve):
            link = [0]

            def chained(ins, l):
                link[0] += 1
                ins.then_inc(dve_link, 1)
                dve.wait_ge(dve_link, l * DVE_LINKS + link[0])

            nc.vector.memset(warm[:, :], 0.0)
            nc.vector.memset(vec_rows[:, :], 0.0).then_inc(rows_clear, 1)
            dve.sem_inc(w_lo_ready, RAW)
            for t in range(T):
                dve.wait_ge(x_landed[t], 16)
                dve.sem_inc(x_ready, 2)
            dve.wait_ge(rows_turned, 1)
            for at, n in VECTORS.items():
                src = bank_x[:, DEPTH * at:DEPTH * (at + n)].rearrange("p (l c) -> p l c", l=DEPTH)
                dst = vec_all[:, :].rearrange("p (l c) -> p l c", l=DEPTH)[:, :, at:at + n]
                ins = nc.vector.tensor_scalar(dst, src, 0.5 if at == BG else 1.0, None, ALU.mult)
            ins.then_inc(rows_clear, 1)
            dve.wait_ge(rows_clear, 2)

            def split_lo(c, l, g=0):
                if c >= NC:
                    return
                dve.wait_ge(w_hi_ready, l * NC + 4 * g + (c + 1))
                nc.vector.tensor_tensor(split_view(w_lo, c), raw[:, c % RAW, 0:chunk_cols(c)], f32(split_view(w_hi, c)),
                                        ALU.subtract).then_inc(w_lo_ready, 1)

            def scale_left(k, t):
                dve.wait_ge(rstd_ready, k * T + (t + 1))
                nc.vector.tensor_scalar(h[:, t, 0:512], xs[:, t, 0:512], rstd[:, t:t + 1], None, ALU.mult).then_inc(h_ready, 1)

            def turned_lo(k, gain):
                for kc in range(KD):
                    dve.wait_ge(h_hi_ready, k * KD + (kc // 2 * 2 + 2))
                    src = turn_banks[kc // 2][:, (kc % 2) * SEQ:(kc % 2 + 1) * SEQ]
                    nc.vector.scalar_tensor_tensor(out=act_lo[:, kc, :], in0=src, scalar=vec[:, gain + kc:gain + kc + 1],
                                                   in1=f32(act_hi[:, kc, :]), op0=ALU.mult,
                                                   op1=ALU.subtract).then_inc(h_lo_ready, 1)

            def residual(k, last_chunk, l, parts=((0, 0), (0, 1), (1, 0), (1, 1))):
                for t, m in parts:
                    if (t, m) == (1, 1):
                        dve.wait_ge(w_used, used_count(l, POS[last_chunk]))
                    else:
                        dve.wait_ge(acc_done, l * 6 + (3 * k + 2 * t + m + 1))
                    xv = xs[:, t, m * 512:(m + 1) * 512]
                    nc.vector.tensor_tensor(xv, xv, bank_acc[:, 2 * t + m, :], ALU.add).then_inc(x_ready, 1)

            qk_a = scratch[:, 0:T * 384].rearrange("p (t c) -> p t c", t=T)
            rot_a = scratch[:, T * 384:2 * T * 384].rearrange("p (t c) -> p t c", t=T)

            def a_squares(l):
                dve.wait_ge(in_act, l * IN_N + 2)
                dve.wait_ge(in_dve, l * IN_N + 2)
                chained(nc.vector.tensor_tensor(qk_a, qkv[:, :, AQ:AV], qkv[:, :, AQ:AV], ALU.mult), l)
                nc.vector.tensor_reduce(ss_a[:, :, :].rearrange("p t h -> p (t h)"),
                                        qk_a.rearrange("p t (h d) -> p (t h) d", d=HD), AX, ALU.add).then_inc(ss_a_ready, 1)

            def a_norm(l):
                dve.wait_ge(rs_a_ready, l + 1)
                dve.wait_ge(gains_landed, l * 32 + 32)
                dve.wait_ge(in_dve, l * IN_N + 2)
                for t in range(T):
                    src, dst = (v[:, t, :].rearrange("p (h d) -> p h d", d=HD) for v in (qkv[:, :, AQ:AV], qk_a))
                    for a, b, step, to in ((0, 4, 2, 0), (1, 4, 2, 2), (4, 6, 1, 4)):
                        scale = rs_a[:, t, a:b:step]
                        ins = nc.vector.tensor_tensor(dst[:, to:to + 2, :], src[:, a:b:step, :],
                                                      scale.unsqueeze(2).to_broadcast([P, 2, HD]), ALU.mult)
                chained(ins, l)
                for t in range(T):
                    v = qk_a[:, t, :].rearrange("p (h d) -> p h d", d=HD)
                    for m, (a, b) in enumerate(((0, 4), (4, 6))):
                        ins = nc.vector.tensor_tensor(v[:, a:b, :], v[:, a:b, :],
                                                      gain_qk[:, m, :].unsqueeze(1).to_broadcast([P, b - a, HD]), ALU.mult)
                chained(ins, l)

            def a_rotate(l):
                dve.wait_ge(cst_landed, 16)
                for t in range(T):
                    v = qk_a[:, t, :]
                    r = rot_a[:, t, :]
                    v5 = v.rearrange("p (h a s d) -> p h a s d", h=6, a=2, s=2)
                    r5 = r.rearrange("p (h a s d) -> p h a s d", h=6, a=2, s=2)
                    s5 = sin_a[:, t, :].rearrange("p (a s d) -> p a s d", a=2, s=2)
                    for s in range(2):
                        ins = nc.vector.tensor_tensor(r5[:, :, :, s, :], v5[:, :, :, 1 - s, :],
                                                      s5[:, :, s, :].unsqueeze(1).to_broadcast([P, 6, 2, HD // 4]), ALU.mult)
                chained(ins, l)
                for t in range(T):
                    v = qk_a[:, t, :].rearrange("p (h d) -> p h d", d=HD)
                    ins = nc.vector.tensor_tensor(v, v, cos_a[:, t, :].unsqueeze(1).to_broadcast([P, 6, HD]), ALU.mult)
                chained(ins, l)
                nc.vector.tensor_tensor(qkv[:, :, AQ:AV], qk_a, rot_a, ALU.add).then_inc(a_ready, 1)

            sq_d = scratch[:, 0:T * (QR + KVR)].rearrange("p (t c) -> p t c", t=T)

            def c_order(l):
                dve.wait_ge(in_act, l * IN_N + IN_N)
                dve.wait_ge(in_dve, l * IN_N + IN_N)
                for t in range(T):
                    ins = nc.vector.tensor_copy(cq_order[:, t].rearrange("p (g u d) -> p g u d", g=2, u=2),
                                                qkv[:, t, CQ:CK].rearrange("p (u g d) -> p g u d", u=2, g=2))
                ins.then_inc(cq_ready, 1)

            def d_squares(l):
                dve.wait_ge(in_act, l * IN_N + IN_N)
                dve.wait_ge(a_ready, l + 1)
                dve.wait_ge(in_dve, l * IN_N + IN_N)
                chained(nc.vector.tensor_tensor(sq_d, qkv[:, :, DCQ:DKR], qkv[:, :, DCQ:DKR], ALU.mult), l)
                nc.vector.tensor_reduce(ss_d[:, :, 0], sq_d[:, :, 0:QR], AX, ALU.add)
                nc.vector.tensor_reduce(ss_d[:, :, 1], sq_d[:, :, QR:QR + KVR], AX, ALU.add).then_inc(ss_d_ready, 1)

            def d_norm(l):
                dve.wait_ge(rs_d_ready, l + 1)
                for t in range(T):
                    for k, (a, b) in enumerate(((DCQ, DCKV), (DCKV, DKR))):
                        v = qkv[:, t, a:b]
                        ins = nc.vector.tensor_scalar(v, v, rs_d[:, t, k:k + 1], None, ALU.mult)
                ins.then_inc(lat_ready, 1)

            def d_rotate(l):
                dve.wait_ge(x_evac, l * NX + (X_JOBS.index("ukv1") + 1))
                half = ROPE // 2
                rq = tmp[:, 0, 0:T * H * ROPE].rearrange("p (t h d) -> p t h d", t=T, h=H)
                q = qd[:, :, :, HD:DQ]
                k = qkv[:, :, DKR:IN_W]
                rk = tmp[:, 0, T * H * ROPE:T * H * ROPE + T * ROPE].rearrange("p (t d) -> p t d", t=T)
                for s in range(2):
                    a, b = slice(s * half, (s + 1) * half), slice((1 - s) * half, (2 - s) * half)
                    nc.vector.tensor_tensor(rq[:, :, :, a], q[:, :, :, b],
                                            sin_d[:, :, a].unsqueeze(2).to_broadcast([P, T, H, half]), ALU.mult)
                    nc.vector.tensor_tensor(rk[:, :, a], k[:, :, b], sin_d[:, :, a], ALU.mult)
                ins = nc.vector.tensor_tensor(krot[:, :, :], k, cos_d, ALU.mult)
                chained(ins, l)
                nc.vector.tensor_tensor(q, q, cos_d.unsqueeze(2).to_broadcast([P, T, H, ROPE]), ALU.mult)
                ins = nc.vector.tensor_tensor(krot[:, :, :], krot[:, :, :], rk, ALU.add)
                chained(ins, l)
                chained(nc.vector.tensor_tensor(q, q, rq, ALU.add), l)
                nc.vector.tensor_copy(kd[:, :, :, HD:DQ], krot[:, :, :].unsqueeze(2).to_broadcast([P, T, H, ROPE])).then_inc(d_ready, 1)

            def maxima(i, l):
                n, hd, _, _ = HEADS[i]
                b = i % 2
                s = bank_acc[:, b, :]
                dve.wait_ge(scored, l * NH + (i + 1))
                scale = (DQ if n == 3 else HD) ** -0.5
                if n == 2:
                    slope = 2.0 ** (-8.0 * (hd + 1) / H)
                    chained(nc.vector.scalar_tensor_tensor(out=s, in0=dist, scalar=-slope / scale, in1=s,
                                                           op0=ALU.mult, op1=ALU.add), l)
                chained(nc.vector.tensor_reduce(top[:, b, :], s.rearrange("p (t s) -> p t s", t=T), AX, ALU.max), l)
                if n == 2:
                    dve.wait_ge(nsink_ready, l + 1)
                    ins = nc.vector.scalar_tensor_tensor(out=ntop[:, b, :], in0=top[:, b, :], scalar=-scale,
                                                         in1=nsink[:, hd:hd + 1].to_broadcast([P, T]),
                                                         op0=ALU.mult, op1=ALU.min)
                else:
                    ins = nc.vector.tensor_scalar(ntop[:, b, :], top[:, b, :], -scale, None, ALU.mult)
                ins.then_inc(top_ready, 1)

            def normalise(i, l):
                n, _, _, _ = HEADS[i]
                b = i % 2
                dve.wait_ge(exp_ready, l * NH + (i + 1))
                if n == 2:
                    chained(nc.vector.tensor_tensor(psum_p[:, b, :], psum_p[:, b, :], esink[:, b, :], ALU.add), l)
                chained(nc.vector.reciprocal(rsum[:, b, :], psum_p[:, b, :]), l)
                for t in range(T):
                    ins = nc.vector.tensor_scalar(prob[:, b, t, :], prob[:, b, t, :], rsum[:, b, t:t + 1], None, ALU.mult)
                ins.then_inc(prob_ready, 1)

            def heads_lo(i, l):
                n, _, blk, half = HEADS[i]
                if half == 0:
                    return
                dve.wait_ge(o_hi_ready, l * (NH // 2) + (i // 2 + 1))
                nc.vector.tensor_tensor(part_lo[:, n % 2, blk, :], bank_o[:, blk * SEQ:(blk + 1) * SEQ],
                                        f32(part_hi[:, n % 2, blk, :]), ALU.subtract).then_inc(o_lo_ready, 1)

            def mix_lo(q, l):
                dve.wait_ge(mix_hi_ready, l * 4 + (q + 1))
                v = [a[:, 2 * q:2 * q + 2, :].rearrange("p k s -> p (k s)") for a in (act_hi, act_lo)]
                nc.vector.scalar_tensor_tensor(out=v[1], in0=mix[:, q, :], scalar=0.5, in1=f32(v[0]), op0=ALU.mult,
                                               op1=ALU.subtract).then_inc(mix_lo_ready, 1)

            def branch(n, l, quarters):
                dve.wait_ge(gate_tanh, l * GATE_N + (4 * n + 4))
                for q in quarters:
                    if q < 3:
                        dve.wait_ge(y_done, l * 12 + (3 * n + q + 1))
                    else:
                        dve.wait_ge(w_used, used_count(l, POS["y", n]))
                    y = bank_w[:, W_AT["y", n, q] % 2, :]
                    g = big[:, (4 * n + q) % 8, :]
                    if n == 0:
                        nc.vector.scalar_tensor_tensor(out=mix[:, q, :], in0=g, scalar=1.0, in1=y, op0=ALU.add,
                                                       op1=ALU.mult).then_inc(y_read, 1)
                        continue
                    k = 4 * (n - 1) + q
                    if k >= 2:
                        dve.wait_ge(mixed, l * 12 + (k - 1))
                    nc.vector.scalar_tensor_tensor(out=tmp[:, k % 2, :], in0=g, scalar=1.0, in1=y, op0=ALU.add,
                                                   op1=ALU.mult).then_inc(y_read, 1)
                    if n == NB - 1 and q:
                        mix_lo(q - 1, l)

            def mlp(i, l, g=0):
                b = i % 2
                dve.wait_ge(relu_ready, l * FF_N + 2 * g + (i + 1))
                nc.vector.tensor_tensor(sq[b], relu[b], relu[b], ALU.mult).then_inc(u_squared, 1)
                dve.wait_ge(u_squared, l * FF_N + 2 * g + (i + 1))
                dve.wait_ge(u_hi_ready, l * FF_N + 2 * g + (i + 1))
                nc.vector.tensor_tensor(part_lo[:, b, :, :].rearrange("p k s -> p (k s)"), sq[b],
                                        f32(part_hi[:, b, :, :].rearrange("p k s -> p (k s)")),
                                        ALU.subtract).then_inc(u_lo_ready, 1)

            with dve.Fori(0, DEPTH) as l:
                chained(nc.vector.tensor_copy(vec[:, :], vec_all[:, bass.ds(l * NCOL, NCOL)]), l)
                scale_left(2 * l, 0)
                split_lo(0, l)
                scale_left(2 * l, 1)
                turned_lo(2 * l, G1)
                split_lo(1, l)
                split_lo(2, l)
                for s in range(STEPS):
                    kind, j = CHUNKS[s]
                    if s == 2:
                        a_squares(l)
                    if 0 <= s - SOFTMAX < NH:
                        maxima(s - SOFTMAX, l)
                    if 0 <= s - HEAD_OUT < NH:
                        heads_lo(s - HEAD_OUT, l)
                    if kind == "y":
                        branch(j, l, (0, 1))
                    if kind == "in":
                        dve.wait_ge(w_used, used_count(l, j))
                        nc.vector.tensor_copy(qkv[:, 1, j * IN_C:(j + 1) * IN_C], bank_w[:, 1, 0:IN_C]).then_inc(in_dve, 1)
                    if s == 3:
                        a_norm(l)
                    if s == 4:
                        a_rotate(l)
                    if kind != "y":
                        split_lo(s + AHEAD, l)
                    if 0 <= s - SOFTMAX < NH:
                        normalise(s - SOFTMAX, l)
                    if kind == "y":
                        branch(j, l, (2, 3))
                        split_lo(s + AHEAD, l)
                    if s == 8:
                        c_order(l)
                        d_squares(l)
                    if s == 9:
                        d_norm(l)
                    if s == 17:
                        d_rotate(l)
                mix_lo(3, l)
                split_lo(POS["o", 3], l)
                residual(0, ("o", 3), l, ((0, 0),))
                split_lo(POS["f1", 0], l)
                residual(0, ("o", 3), l, ((0, 1),))
                scale_left(2 * l + 1, 0)
                residual(0, ("o", 3), l, ((1, 0), (1, 1)))
                scale_left(2 * l + 1, 1)
                split_lo(POS["f1", 1], l)
                turned_lo(2 * l + 1, G2)
                split_lo(POS["f2", 0], l)
                mlp(0, l)
                with dve.Fori(0, MLP_TURNS) as g:
                    for i in (1, 2):
                        split_lo(POS["f1", i] + AHEAD - 1, l, g)
                        mlp(i, l, g)
                        split_lo(POS["f2", i - 1] + AHEAD - 1, l, g)
                split_lo(POS["f2", FF_N - 1], l)
                mlp(FF_N - 1, l)
                residual(1, ("f2", FF_N - 1), l)
                used = link[0]
            assert used == DVE_LINKS, used
            dve.wait_ge(final_g_landed, 16)
            for t in range(T):
                dve.wait_ge(rstd_ready, 2 * T * DEPTH + t + 1)
                for m in range(2):
                    half = slice(m * 512, (m + 1) * 512)
                    nc.vector.scalar_tensor_tensor(out=h[:, t, half], in0=xs[:, t, half], scalar=rstd[:, t:t + 1],
                                                   in1=scratch[:, half], op0=ALU.mult, op1=ALU.mult).then_inc(h_ready, 1)

        @block.tensor
        def _(pe):
            pe.sem_inc(w_used, RING)
            pe.wait_ge(ident_landed, 16)
            pe.wait_ge(rows_landed, 16 * 3)
            pe.wait_ge(d_rows_landed, 16 * 3)
            nc.tensor.transpose(bank_x[:, 0:DEPTH * NCOL], vec_rows[:, :],
                                ident[0:DEPTH * NCOL, 0:DEPTH * NCOL]).then_inc(rows_turned, 1)

            def split_product(dst, sides, start, stop, ready=None):
                for k, (s_hi, s_lo, m_hi, m_lo) in enumerate(sides):
                    if ready is not None:
                        pe.wait_ge(h_lo_ready, ready + (k + 1))
                    first, last = start and k == 0, stop and k == len(sides) - 1
                    nc.tensor.matmul(dst, s_hi, m_hi, start=first, stop=False)
                    nc.tensor.matmul(dst, s_hi, m_lo, start=False, stop=False)
                    ins = nc.tensor.matmul(dst, s_lo, m_hi, start=False, stop=last)
                return ins

            def keep_warm(n):
                for _ in range(n):
                    nc.tensor.matmul(bank_w[:, 1, 0:P], ident, ident, start=True, stop=True)

            def turn_h(k):
                for t in range(T):
                    keep_warm(WARM[t])
                    pe.wait_ge(h_ready, k * T + (t + 1))
                    for kc in range(KD):
                        if kc == KD // 2:
                            pe.wait_ge(h_right_ready, k * T + (t + 1))
                        at = (kc % 2) * SEQ + t * P
                        ins = nc.tensor.transpose(turn_banks[kc // 2][:, at:at + P], h[:, t, kc * P:(kc + 1) * P], ident)
                        if t == T - 1 and kc % 2 == 1:
                            ins.then_inc(h_turned, 1)

            def small(step, l):
                name = X_STEP.get(step)
                if name is None:
                    return
                k = X_JOBS.index(name)
                if k:
                    pe.wait_ge(x_evac, l * NX + k)
                x4 = bank_x[:, :].rearrange("p (b t s) -> p b t s", b=2, t=T)
                if name == "aq":
                    pe.wait_ge(a_ready, l + 1)
                if name == "bq":
                    pe.wait_ge(in_act, l * IN_N + -(-BV // IN_C))
                    pe.wait_ge(in_dve, l * IN_N + -(-BV // IN_C))
                if name == "ck":
                    pe.wait_ge(in_act, l * IN_N + IN_N)
                    pe.wait_ge(in_dve, l * IN_N + IN_N)
                if name == "cq":
                    pe.wait_ge(cq_ready, l + 1)
                if name == "lq":
                    pe.wait_ge(lat_ready, l + 1)
                if name == "uq0":
                    pe.wait_ge(lat_landed, l * 48 + 48)
                if name == "dq0":
                    pe.wait_ge(d_ready, l + 1)
                if name in ("aq", "bq", "bk", "cq"):
                    src = {"aq": qkv[:, :, AQ:AK], "bq": qkv[:, :, BQ:BK], "bk": qkv[:, :, BK:BV], "cq": cq_order}[name]
                    for t in range(T):
                        for g in range(2):
                            ins = nc.tensor.transpose(x4[:, g, t, :], src[:, t, g * P:(g + 1) * P], ident)
                elif name in ("ak", "ck", "lkv"):
                    a = {"ak": AK, "ck": CK, "lkv": DCKV}[name]
                    for t in range(T):
                        ins = nc.tensor.transpose(x4[:, 0, t, :], qkv[:, t, a:a + P], ident)
                elif name == "lq":
                    for t in range(T):
                        nc.tensor.transpose(x4[:, 0, t, :], qkv[:, t, DCQ:DCQ + P], ident)
                        ins = nc.tensor.transpose(x4[0:QR - P, 1, t, :], qkv[:, t, DCQ + P:DCKV], ident)
                elif name in ("uq0", "uq1"):
                    t = int(name[-1])
                    nc.tensor.matmul(bank_x[:, 0:H * DQ], latT[:, 0, t * P:(t + 1) * P], w_uq[:, 0, :], start=True, stop=False)
                    ins = nc.tensor.matmul(bank_x[:, 0:H * DQ], latT[0:QR - P, 1, t * P:(t + 1) * P],
                                           w_uq[0:QR - P, 1, :], start=False, stop=True)
                elif name in ("ukv0", "ukv1"):
                    t = int(name[-1])
                    ins = nc.tensor.matmul(bank_x[:, :], latT[:, 2, t * P:(t + 1) * P], w_ukv[:, :], start=True, stop=True)
                else:
                    src, g = (qd if name[1] == "q" else kd), int(name[-1])
                    for u in range(2):
                        for t in range(T):
                            ins = nc.tensor.transpose(x4[0:DQ, u, t, :], src[:, t, 2 * g + u, :], ident)
                ins.then_inc(x_turned, 1)

            def scores(i, l):
                n, hd, blk, half = HEADS[i]
                b = i % 2
                if i >= 2:
                    pe.wait_ge(exp_ready, l * NH + (i - 1))
                job = {0: "ak", 1: "bk", 2: "ck", 3: "dk1" if blk else "dk0"}[n]
                pe.wait_ge(x_evac, l * NX + (X_JOBS.index(job) + 1))
                if n == 3:
                    q, k = qT[3][0:DQ, 2 * blk + half, :], kT[3][0:DQ, 2 * blk + half, :]
                else:
                    rows = slice(half * HD, (half + 1) * HD)
                    q, k = qT[n][rows, blk, :], kT[n][rows, blk if n == 1 else 0, :]
                if n == 1:
                    pe.wait_ge(bias_ready, l + 1)
                for t in range(T):
                    keys = slice(t * SEQ, (t + 1) * SEQ)
                    if n == 1:
                        nc.tensor.matmul(bank_acc[:, b, keys], flip, bias[:, hd, keys], start=True, stop=False)
                    ins = nc.tensor.matmul(bank_acc[:, b, keys], q[:, t * P:(t + 1) * P], k, start=(n != 1), stop=True)
                ins.then_inc(scored, 1)

            def turn_prob(i, l):
                b = i % 2
                pe.wait_ge(prob_ready, l * NH + (i + 1))
                if i >= 2:
                    pe.wait_ge(probT_ready, l * NH + (i - 1))
                for kt in range(T):
                    for t in range(T):
                        at = kt * SEQ + t * P
                        ins = nc.tensor.transpose(bank_acc[:, 2 + b, at:at + P], prob[:, b, t, kt * P:(kt + 1) * P], ident)
                ins.then_inc(prob_turned, 1)

            def values(i, l):
                n, hd, blk, half = HEADS[i]
                pe.wait_ge(probT_ready, l * NH + (i + 1))
                if i >= 2 and half == 0:
                    pe.wait_ge(o_lo_ready, l * (NH // 2) + i // 2)
                for kt in range(T):
                    if n == 3:
                        v = vd[:, kt, hd, :]
                    else:
                        a = {0: AV + half * HD, 1: BV + hd * HD, 2: CV + half * HD}[n]
                        v = qkv[:, kt, a:a + HD]
                    ins = nc.tensor.matmul(bank_o[half * HD:(half + 1) * HD, blk * SEQ:(blk + 1) * SEQ], v,
                                           probT[:, i % 2, kt, :], start=(kt == 0), stop=(kt == T - 1))
                ins.then_inc(pv_done, 1)

            def project(j, l):
                pe.wait_ge(w_lo_ready, lo_count(l, j))
                hi, lo = k_view(w_hi, j, KD), k_view(w_lo, j, KD)
                for t in range(T):
                    if j:
                        pe.wait_ge((in_act, in_dve)[t], l * IN_N + j)
                    tok = slice(t * P, (t + 1) * P)
                    sides = [(act_hi[:, kc, tok], act_lo[:, kc, tok], hi[:, kc, :], lo[:, kc, :]) for kc in range(KD)]
                    ins = split_product(bank_w[:, t, 0:IN_C], sides, True, True, 2 * l * KD if j == 0 and t == 0 else None)
                    ins.then_inc(w_used if t == T - 1 else in_half, 1)

            def bank_free(job, l):
                k = W_AT[job]
                if k < 2:
                    pe.wait_ge((in_act, in_dve)[k], l * IN_N + IN_N)
                    return
                kind, n, q = W_JOBS[k - 2]
                if kind == "gate":
                    pe.wait_ge(gate_tanh, l * GATE_N + (n + 1))
                else:
                    pe.wait_ge(y_read, l * 16 + (4 * n + q + 1))

            def feature_blocks(bank, c, ready=None):
                hi, lo = k_view(w_hi, c, KD), k_view(w_lo, c, KD)
                for d in range(2):
                    sides = [(hi[:, kc, d * P:(d + 1) * P], lo[:, kc, d * P:(d + 1) * P], act_hi[:, kc, :], act_lo[:, kc, :])
                             for kc in range(KD)]
                    ins = split_product(bank[:, d * SEQ:(d + 1) * SEQ], sides, True, True, ready if d == 0 else None)
                ins.then_inc(w_used, 1)

            def gate(i, l):
                bank_free(("gate", i, 0), l)
                pe.wait_ge(w_lo_ready, lo_count(l, POS["gate", i]))
                feature_blocks(bank_w[:, W_AT["gate", i, 0] % 2, :], POS["gate", i])

            def branch(n, l):
                c = POS["y", n]
                pe.wait_ge(w_lo_ready, lo_count(l, c))
                pe.wait_ge(o_lo_ready, l * (NH // 2) + (2 * n + 2))
                hi, lo = k_view(w_hi, c, 2), k_view(w_lo, c, 2)
                for q in range(4):
                    bank_free(("y", n, q), l)
                    for d in range(2):
                        f = slice((2 * q + d) * P, (2 * q + d + 1) * P)
                        sides = [(hi[:, k, f], lo[:, k, f], part_hi[:, n % 2, k, :], part_lo[:, n % 2, k, :]) for k in range(2)]
                        ins = split_product(bank_w[:, W_AT["y", n, q] % 2, d * SEQ:(d + 1) * SEQ], sides, True, True)
                    ins.then_inc(y_done if q < 3 else w_used, 1)

            def token_sum(c, a_hi, a_lo, t, m, start, stop):
                hi, lo = k_view(w_hi, c, 2), k_view(w_lo, c, 2)
                tok, half = slice(t * P, (t + 1) * P), slice(m * 512, (m + 1) * 512)
                sides = [(a_hi[:, k, tok], a_lo[:, k, tok], hi[:, k, half], lo[:, k, half]) for k in range(2)]
                return split_product(bank_acc[:, 2 * t + m, :], sides, start, stop)

            def mlp_in(i, l, g=0):
                c = POS["f1", i]
                if i >= 2:
                    pe.wait_ge(relu_ready, l * FF_N + 2 * g + (i - 1))
                pe.wait_ge(w_lo_ready, lo_count(l, c, g))
                feature_blocks(bank_w[:, i % 2, :], c, (2 * l + 1) * KD if i == 0 else None)

            def mlp_out(i, l, g=0):
                c = POS["f2", i]
                pe.wait_ge(w_lo_ready, lo_count(l, c, g))
                pe.wait_ge(u_lo_ready, l * FF_N + 2 * g + (i + 1))
                for t in range(T):
                    for m in range(2):
                        ins = token_sum(c, part_hi[:, i % 2], part_lo[:, i % 2], t, m, i == 0, False)
                ins.then_inc(w_used, 1)

            def mlp_out_last(l):
                a, b = FF_N - 2, FF_N - 1
                for i, t, m in ((a, 0, 0), (a, 0, 1), (b, 0, 0), (b, 0, 1), (a, 1, 0), (b, 1, 0), (a, 1, 1), (b, 1, 1)):
                    c = POS["f2", i]
                    if (t, m) == (0, 0):
                        pe.wait_ge(w_lo_ready, lo_count(l, c))
                        pe.wait_ge(u_lo_ready, l * FF_N + (i + 1))
                    ins = token_sum(c, part_hi[:, i % 2], part_lo[:, i % 2], t, m, False, i == b)
                    if (t, m) == (1, 1):
                        ins.then_inc(w_used, 1)
                    elif i == b:
                        ins.then_inc(acc_done, 1)

            with pe.Fori(0, DEPTH) as l:
                turn_h(2 * l)
                keep_warm(WARM[T])
                for s in range(STEPS):
                    kind, j = CHUNKS[s]
                    small((s, 0), l)
                    if kind == "in":
                        project(j, l)
                    if kind == "gate":
                        gate(j, l)
                    if kind == "y":
                        branch(j, l)
                    small((s, 1), l)
                    if 0 <= s - SCORES < NH:
                        scores(s - SCORES, l)
                    if 0 <= s - TURN < NH:
                        turn_prob(s - TURN, l)
                    if 0 <= s - VALUES < NH:
                        values(s - VALUES, l)
                parts = [(t, m) for t in range(T) for m in range(2)]

                def w_o_sum(c, t, m):
                    if (t, m) == (0, 0):
                        pe.wait_ge(mix_lo_ready, l * 4 + (c + 1))
                        pe.wait_ge(w_lo_ready, lo_count(l, POS["o", c]))
                    ins = token_sum(POS["o", c], act_hi[:, 2 * c:2 * c + 2], act_lo[:, 2 * c:2 * c + 2], t, m,
                                    c == 0, c == 3)
                    if (t, m) == parts[-1]:
                        ins.then_inc(w_used, 1)
                    elif c == 3:
                        ins.then_inc(acc_done, 1)

                for c in range(2):
                    for t, m in parts:
                        w_o_sum(c, t, m)
                for t, m in parts:
                    for c in range(2, 4):
                        w_o_sum(c, t, m)
                turn_h(2 * l + 1)
                keep_warm(WARM[T])
                mlp_in(0, l)
                mlp_in(1, l)
                mlp_out(0, l)
                mlp_in(2, l)
                with pe.Fori(0, MLP_TURNS - 1) as g:
                    mlp_out(1, l, g)
                    mlp_in(3, l, g)
                    mlp_out(2, l, g)
                    mlp_in(4, l, g)
                mlp_out(FF_N - 3, l)
                mlp_in(FF_N - 1, l)
                mlp_out_last(l)


_INS = ["x", "norm1_g", "w_in", "w_gate", "b_gate", "a_q_norm_g", "a_k_norm_g", "b_rel_bias", "c_sink", "d_q_norm_g",
        "d_kv_norm_g", "d_w_uq", "d_w_ukv", "w_branch", "w_o", "norm2_g", "w_ff1", "w_ff2", "final_g"]


def kernel(**inputs):
    import concourse.bacc as bacc
    from concourse.bass_utils import run_bass_kernel_spmd

    nc = bacc.Bacc("TRN2", target_bir_lowering=False, num_devices=1)
    arrays = {f"in_{n}": np.ascontiguousarray(inputs[n]) for n in _INS}
    arrays["in_table"] = constants()
    args = [nc.dram_tensor(n, a.shape, mybir.dt.from_np(a.dtype), kind="ExternalInput").ap() for n, a in arrays.items()]
    args.append(nc.dram_tensor("out_y", (1, SEQ, D), F32, kind="ExternalOutput").ap())
    trunk_kernel(nc, *args)
    r = run_bass_kernel_spmd(nc, [arrays], core_ids=[0])
    return r.results[0]["out_y"]
```
